# Optimizing a Trainium2 kernel written in Bass

```python
import jax, jax.numpy as jnp
from jax import lax
import numpy as np

D_MODEL = 1024
BATCH = 1
SEQ = 512
DEPTH = 1

CHUNK = 64
MIX_WIDTH = D_MODEL
HEAD_DIM = 64
CONV_WIDTH = MIX_WIDTH // 2
RWKV_WIDTH = MIX_WIDTH - CONV_WIDTH
CONV_GROUPS = CONV_WIDTH // HEAD_DIM
RWKV_HEADS = RWKV_WIDTH // HEAD_DIM
CONV_K = 3
DECAY_LORA = 64
AAA_LORA = 64
GATE_LORA = 128
N_EXPERTS = 32
TOP_K = 4
D_FF = D_MODEL
SWIGLU_LIMIT = 7.0
SWIGLU_ALPHA = 1.702
MOE_BLOCK = 128
NORM_EPS = 1e-5
GN_EPS = HEAD_DIM * 1e-5

CONV_COLS = 3 * CONV_WIDTH
RWKV_COLS = 3 * RWKV_WIDTH + DECAY_LORA + AAA_LORA + GATE_LORA
IN_COLS = CONV_COLS + RWKV_COLS

kernel_name = "hymba_conv_rwkv7_moe_encoder"

def rms_norm(x, g):
    xf = x.astype(jnp.float32)
    y = xf * lax.rsqrt(jnp.mean(xf * xf, axis=-1, keepdims=True) + NORM_EPS)
    return (y * g.astype(jnp.float32)).astype(x.dtype)

def group_rms_norm(y, g, groups):
    lead = y.shape[:-1]
    yf = y.astype(jnp.float32).reshape(*lead, groups, -1)
    yf = yf * lax.rsqrt(jnp.mean(yf * yf, axis=-1, keepdims=True) + NORM_EPS)
    return (yf.reshape(*lead, -1) * g.astype(jnp.float32)).astype(y.dtype)

def token_shift_lerp(p, mu):
    prev = jnp.pad(p, ((0, 0), (1, 0), (0, 0)))[:, :-1]
    return p + (prev - p) * mu

def causal_depthwise_conv(z, w):
    C = z.shape[-1]
    return lax.conv_general_dilated(
        z, w.reshape(CONV_K, 1, C).astype(z.dtype), window_strides=(1,),
        padding=[(CONV_K - 1, 0)], dimension_numbers=("NWC", "WIO", "NWC"),
        feature_group_count=C)

def short_conv_mixer(p, conv_w, conv_norm_g):
    u, b_gate, c_gate = jnp.split(p, 3, axis=-1)
    y = b_gate * causal_depthwise_conv(c_gate * u, conv_w)
    return group_rms_norm(y, conv_norm_g, CONV_GROUPS)

def wkv7_scan(r, w, k, v, kk, a):
    B_, S_, H, N = r.shape
    n_chunks = S_ // CHUNK

    def to_chunks(t):
        return t.reshape(B_, n_chunks, CHUNK, H, N).transpose(1, 2, 0, 3, 4)

    def frame_step(state, inp):
        r_t, w_t, k_t, v_t, kk_t, a_t = inp
        sa = jnp.einsum("bhvk,bhk->bhv", state, -kk_t)
        state = (state * w_t[:, :, None, :]
                 + sa[..., None] * (kk_t * a_t)[:, :, None, :]
                 + v_t[..., None] * k_t[:, :, None, :])
        return state, jnp.einsum("bhvk,bhk->bhv", state, r_t)

    def chunk_step(state, chunk_inp):
        return lax.scan(frame_step, state, chunk_inp)

    state0 = jnp.zeros((B_, H, N, N), jnp.float32)
    _, out = lax.scan(chunk_step, state0, tuple(to_chunks(t) for t in (r, w, k, v, kk, a)))
    return out.transpose(2, 0, 1, 3, 4).reshape(B_, S_, H, N)

def rwkv7_mixer(p, mu, w0, w_up, a0, a_up, g_up, k_k, k_a, r_k, gn_w, gn_b):
    B_, S_, _ = p.shape
    f32 = jnp.float32
    q = token_shift_lerp(p, mu)
    i1 = RWKV_WIDTH
    i2 = 2 * RWKV_WIDTH
    i3 = 3 * RWKV_WIDTH
    i4 = i3 + DECAY_LORA
    i5 = i4 + AAA_LORA
    r, k, v, dw, da, dg = jnp.split(q, [i1, i2, i3, i4, i5], axis=-1)
    w_log = -jax.nn.softplus(-(w0 + jnp.tanh(dw) @ w_up).astype(f32)) - 0.5
    decay = jnp.exp(-jnp.exp(w_log))
    a = jax.nn.sigmoid((a0 + da @ a_up).astype(f32))
    g = jax.nn.sigmoid(dg) @ g_up

    def heads(t):
        return t.astype(f32).reshape(B_, S_, RWKV_HEADS, HEAD_DIM)

    kk = heads(k * k_k)
    kk = kk / jnp.maximum(jnp.linalg.norm(kk, axis=-1, keepdims=True), 1e-12)
    k_mod = k.astype(f32) * (1.0 + (a - 1.0) * k_a.astype(f32))
    r_h, k_h, v_h = heads(r), heads(k_mod), heads(v)
    a_h, w_h = heads(a), heads(decay)
    o = wkv7_scan(r_h, w_h, k_h, v_h, kk, a_h)
    mean = jnp.mean(o, axis=-1, keepdims=True)
    var = jnp.mean(jnp.square(o - mean), axis=-1, keepdims=True)
    o = ((o - mean) * lax.rsqrt(var + GN_EPS)).reshape(B_, S_, RWKV_WIDTH)
    o = o * gn_w.astype(f32) + gn_b.astype(f32)
    bonus = jnp.sum(r_h * k_h * r_k.astype(f32), axis=-1, keepdims=True) * v_h
    o = o + bonus.reshape(B_, S_, RWKV_WIDTH)
    return (o * g.astype(f32)).astype(p.dtype)

def moe_ffn(h, w_router, b_router, w_gu, b_gu, w_down, b_down):
    B_, S_, D = h.shape
    n_tok = B_ * S_
    t = h.reshape(n_tok, D)
    logits = (t @ w_router + b_router).astype(jnp.float32)
    top_logit, top_e = lax.top_k(logits, TOP_K)
    gates = jax.nn.softmax(top_logit, axis=-1)
    n_assign = n_tok * TOP_K
    flat_e = top_e.reshape(n_assign).astype(jnp.int32)
    flat_tok = jnp.arange(n_assign, dtype=jnp.int32) // TOP_K
    order = jnp.argsort(flat_e)
    sorted_e = flat_e[order]
    counts = jnp.bincount(flat_e, length=N_EXPERTS).astype(jnp.int32)
    padded = (counts + MOE_BLOCK - 1) // MOE_BLOCK * MOE_BLOCK
    pad_end = jnp.cumsum(padded)
    pad_start = pad_end - padded
    start = jnp.cumsum(counts) - counts
    rank = jnp.arange(n_assign, dtype=jnp.int32) - start[sorted_e]
    dest = jnp.zeros((n_assign,), jnp.int32).at[order].set(pad_start[sorted_e] + rank)
    n_slots = n_assign + N_EXPERTS * MOE_BLOCK
    n_blocks = n_slots // MOE_BLOCK
    slot_tok = jnp.full((n_slots,), n_tok, jnp.int32).at[dest].set(flat_tok)
    block_e = jnp.minimum(
        jnp.searchsorted(pad_end, jnp.arange(n_blocks, dtype=jnp.int32) * MOE_BLOCK, side="right"),
        N_EXPERTS - 1).astype(jnp.int32)
    t_pad = jnp.concatenate([t, jnp.zeros((1, D), t.dtype)], axis=0)
    xin = t_pad[slot_tok].reshape(n_blocks, MOE_BLOCK, D)

    def expert_block(args):
        xb, e = args
        gu = xb @ w_gu[e] + b_gu[e]
        gate, up = gu[:, :D_FF], gu[:, D_FF:]
        gate = jnp.minimum(gate, SWIGLU_LIMIT)
        up = jnp.clip(up, -SWIGLU_LIMIT, SWIGLU_LIMIT)
        act = (up + 1.0) * (gate * jax.nn.sigmoid(SWIGLU_ALPHA * gate))
        return act @ w_down[e] + b_down[e]

    y_slots = lax.map(expert_block, (xin, block_e)).reshape(n_slots, D)
    y = y_slots[dest].reshape(n_tok, TOP_K, D)
    out = jnp.einsum("tkd,tk->td", y, gates.astype(y.dtype))
    return out.reshape(B_, S_, D)

def setup_inputs(seed: int = 0) -> dict:
    key = jax.random.key(seed)
    ks = jax.random.split(key, 26)
    f32 = jnp.float32
    L = DEPTH

    def nrm(k, shape, scale):
        return jax.random.normal(k, shape, f32) * scale

    def gain(k, shape):
        return 1.0 + 0.02 * jax.random.normal(k, shape, f32)

    return {
        "x": nrm(ks[0], (BATCH, SEQ, D_MODEL), 1.0),
        "w_in": nrm(ks[1], (L, D_MODEL, IN_COLS), D_MODEL ** -0.5),
        "conv_w": nrm(ks[2], (L, CONV_K, CONV_WIDTH), CONV_K ** -0.5),
        "conv_norm_g": gain(ks[3], (L, CONV_WIDTH)),
        "rwkv_mu": jax.random.uniform(ks[4], (L, RWKV_COLS), f32, 0.0, 1.0),
        "w0": jax.random.uniform(ks[5], (L, RWKV_WIDTH), f32, -6.0, 0.0),
        "w_up": nrm(ks[6], (L, DECAY_LORA, RWKV_WIDTH), 0.5 * DECAY_LORA ** -0.5),
        "a0": nrm(ks[7], (L, RWKV_WIDTH), 0.5),
        "a_up": nrm(ks[8], (L, AAA_LORA, RWKV_WIDTH), 0.5 * AAA_LORA ** -0.5),
        "g_up": nrm(ks[9], (L, GATE_LORA, RWKV_WIDTH), GATE_LORA ** -0.5),
        "k_k": 0.85 + 0.05 * jax.random.normal(ks[10], (L, RWKV_WIDTH), f32),
        "k_a": 1.0 + 0.05 * jax.random.normal(ks[11], (L, RWKV_WIDTH), f32),
        "r_k": nrm(ks[12], (L, RWKV_HEADS, HEAD_DIM), 0.1),
        "gn_w": gain(ks[13], (L, RWKV_WIDTH)),
        "gn_b": nrm(ks[14], (L, RWKV_WIDTH), 0.01),
        "w_out": nrm(ks[15], (L, MIX_WIDTH, D_MODEL), MIX_WIDTH ** -0.5),
        "norm_mix_g": gain(ks[16], (L, D_MODEL)),
        "norm_ffn_g": gain(ks[17], (L, D_MODEL)),
        "w_router": nrm(ks[18], (L, D_MODEL, N_EXPERTS), D_MODEL ** -0.5),
        "b_router": nrm(ks[19], (L, N_EXPERTS), 0.01),
        "w_gu": nrm(ks[20], (L, N_EXPERTS, D_MODEL, 2 * D_FF), D_MODEL ** -0.5),
        "b_gu": nrm(ks[21], (L, N_EXPERTS, 2 * D_FF), 0.01),
        "w_down": nrm(ks[22], (L, N_EXPERTS, D_FF, D_MODEL), D_FF ** -0.5),
        "b_down": nrm(ks[23], (L, N_EXPERTS, D_MODEL), 0.01),
        "norm_final_g": gain(ks[24], (D_MODEL,)),
    }

def reference(x, w_in, conv_w, conv_norm_g, rwkv_mu, w0, w_up, a0, a_up, g_up, k_k, k_a, r_k,
              gn_w, gn_b, w_out, norm_mix_g, norm_ffn_g, w_router, b_router, w_gu, b_gu,
              w_down, b_down, norm_final_g):
    for l in range(DEPTH):
        h = rms_norm(x, norm_mix_g[l])
        p = h @ w_in[l]
        y_conv = short_conv_mixer(p[..., :CONV_COLS], conv_w[l], conv_norm_g[l])
        y_rwkv = rwkv7_mixer(p[..., CONV_COLS:], rwkv_mu[l], w0[l], w_up[l], a0[l], a_up[l],
                             g_up[l], k_k[l], k_a[l], r_k[l], gn_w[l], gn_b[l])
        y = jnp.concatenate([y_conv, y_rwkv], axis=-1)
        x = x + y @ w_out[l]
        h = rms_norm(x, norm_ffn_g[l])
        x = x + moe_ffn(h, w_router[l], b_router[l], w_gu[l], b_gu[l], w_down[l], b_down[l])
    return rms_norm(x, norm_final_g)


_drawn_inputs = setup_inputs


def setup_inputs(seed=0):
    import zlib

    import numpy as np

    out = dict(_drawn_inputs(seed))
    spreads = {}
    factors = {'gn_b': 3.642, 'b_gu': 8.0, 'b_down': 8.0, 'norm_final_g': 2.855}
    for name, (base, spread) in spreads.items():
        noise = np.random.default_rng([zlib.crc32(name.encode()), seed]).standard_normal(out[name].shape)
        drawn = base * np.exp(spread * noise) if base else spread * noise
        out[name] = __import__('jax').numpy.asarray(drawn.astype(out[name].dtype))
    for name, factor in factors.items():
        out[name] = (out[name] * factor).astype(out[name].dtype)
    return out
```

```python
import concourse.bass as bass
from concourse import mybir
from contextlib import ExitStack

F32 = mybir.dt.float32
BF16 = mybir.dt.bfloat16
I32 = mybir.dt.int32
ALU = mybir.AluOpType
ACT = mybir.ActivationFunctionType
AX = mybir.AxisListType

P = 128
D = 1024
KD = D // P
T = 512
NT = T // P
NJ = 4
C = 64
NCH = T // C
NCP = NCH // 2
NH = 8
E = 32
TOPK = 4
FF = 1024
SLOTS = P
HALF = SLOTS // 2
EXTRA = 16
NBLK = E + EXTRA
NQ = 26
GQ = 2
NG = NQ // GQ
Q_R, Q_K, Q_V, Q_WA, Q_G, Q_U, Q_B, Q_C = 0, 4, 8, 12, 13, 14, 18, 22
PC_GMIX, PC_GFFN, PC_CW, PC_CG, PC_MU = 0, 8, 16, 28, 32
PC_W0, PC_A0, PC_KK, PC_KA, PC_RK, PC_GNW, PC_GNB, PC_N = 46, 50, 54, 58, 62, 66, 70, 74
(M_ID, M_HEAD, M_STRICT, M_INCL, M_TRI, M_ONE, M_L1UP, M_LEV) = 0, 1, 2, 3, 4, 5, 6, 7
LEVELS = (2, 4, 8, 16, 32)
M_PACK = M_LEV + len(LEVELS)
M_SPREAD = M_PACK + 4
M_N = M_SPREAD + 4
EPS = 1e-5
GN_EPS = 64 * 1e-5
DECAY_SCALE = -0.6065306597126334
FAR = 1.0e6


def build(nc, x, w_in, pcol, consts, iota, wa_up, g_up, w_out, w_router, b_router,
          w_gu, b_gu, w_down, b_down, g_final, out):
    h2_dram = nc.dram_tensor("h2_scratch", (T, D), F32, kind="Internal").ap()
    y_dram = nc.dram_tensor("y_scratch", (T * TOPK, D), F32, kind="Internal").ap()
    ctx = ExitStack()
    with ctx:
        def sb(name, shape, dt=F32):
            return ctx.enter_context(nc.sbuf_tensor(name, shape, dt))

        def sem(name):
            return ctx.enter_context(nc.semaphore(name))

        ring = sb("weight_ring", [P, 24 * 1024])
        wgu_sb = ring[:, 0:16384].rearrange("p (k n) -> p k n", k=KD)
        wdn_sb = ring[:, 16384:24576].rearrange("p (k n) -> p k n", k=KD)
        area = sb("work_area", [P, 23 * 1024])
        mats = sb("tables", [P, M_N, P])
        pc = sb("channel_params", [P, PC_N])
        small = sb("small", [P, 64])
        psum = ctx.enter_context(nc.psum_tensor("psum", [P, 8 * 512], F32))

        def bank(b, lo=0, hi=512):
            return psum[:, b * 512 + lo:b * 512 + hi]

        ident = mats[:, M_ID, :]
        head_ones = mats[:, M_HEAD, :]
        ones = mats[:, M_ONE, :]
        eps_c = small[:, 0:1]
        gneps_c = small[:, 1:2]

        xa = area[:, 0:4096].rearrange("p (a n) -> p a n", a=NT)
        at = area[:, 0:2048].rearrange("p (j t) -> p j t", j=NJ)
        bt = area[:, 2048:4096].rearrange("p (j t) -> p j t", j=NJ)
        x_sq = area[:, 8192:12288].rearrange("p (a n) -> p a n", a=NT)
        hT = area[:, 4096:8192].rearrange("p (k t) -> p k t", k=KD)
        oT = hT[:, 0:4, :]
        tmpo = hT[:, 4:8, :]
        pT = area[:, 8192:8192 + NQ * T].rearrange("p (q t) -> p q t", q=NQ)
        y_tiles = [pT[:, q, :] for q in (*range(Q_U, Q_U + NJ), *range(Q_R, Q_R + NJ))]
        o2 = 8192 + NQ * T
        bonus = area[:, o2:o2 + 2048].rearrange("p (j t) -> p j t", j=NJ)
        wbuf = [ring[:, b * 2048:(b + 1) * 2048].rearrange("p (k n) -> p k n", k=KD) for b in range(4)]

        def ringt(chunk, n=1):
            return ring[:, chunk * 2048:(chunk + n) * 2048]

        dbuf = ringt(4).rearrange("p (j t) -> p j t", j=NJ)
        ldec = ringt(5).rearrange("p (j t) -> p j t", j=NJ)
        cdec = ringt(6).rearrange("p (j t) -> p j t", j=NJ)
        e2 = ringt(7).rearrange("p (j t) -> p j t", j=NJ)
        def mat(n):
            return ring[:, 8192 + n * 1024:8192 + (n + 1) * 1024].rearrange("p (s t) -> p s t", s=NH)
        LL, QB, MT, QK, TI, UI, XI, LB = (mat(n) for n in range(8))

        def row(n):
            return ring[:, n * 512:(n + 1) * 512]
        atm, btm, ktm, vtm, mv, u0, wt, sa = (row(n) for n in range(8))
        state = [row(8 + n).rearrange("p (j v) -> p j v", j=NJ) for n in range(3)]
        pcm = [row(11 + n).rearrange("p (j v) -> p j v", j=NJ) for n in range(2)]
        conv_t = row(14)
        conv_rms = row(14)
        scan_rms = pT[:, Q_WA, :]
        tmp_state = row(13).rearrange("p (j v) -> p j v", j=NJ)
        wup = sb("lora_up", [P, 2, T])
        rmask = e2[:, 0, :]
        pend = small[:, 8:8 + NJ * NCH].rearrange("p (j c) -> p j c", j=NJ)
        wout_sb = wdn_sb

        xr = area[:, 0:4096].rearrange("p (a n) -> p a n", a=NT)
        h2T = area[:, 4096:8192].rearrange("p (k t) -> p k t", k=KD)
        xg = area[:, 4096:5120]
        xiT = area[:, 5120:6144].rearrange("p (k s) -> p k s", k=KD)
        yb = area[:, 6144:7168]
        h2 = area[:, 10240:14336].rearrange("p (a n) -> p a n", a=NT)
        gm, sg, up1, actv = (area[:, 8192 + n * 1024:9216 + n * 1024].rearrange("p (h n) -> p h n", h=2)
                             for n in range(4))
        bparts = area[0:3 * E, 19456:20992].bitcast(BF16)
        wr_sb = area[:, 20992:21248].rearrange("p (k e) -> p k e", k=KD)
        lgts = area[0:E, 17408:17920]
        sel4 = area[:, 17920:18432].rearrange("p (a s) -> p a s", a=NT)
        slot_id = area[:, 18432:18560]
        actT = area[:, 12288:13312].rearrange("p (k s) -> p k s", k=KD)
        NS = NT * E
        (lg, blk1, rmod1, gate, krank, t_a, t_b, t_c, sel, rank, psel, t_d) = (
            area[:, 14336 + n * NS:14336 + (n + 1) * NS].rearrange("p (a e) -> p a e", a=NT) for n in range(12))
        extab = [area[:, 15872 + n * 512:16384 + n * 512].rearrange("p (j e) -> p j e", j=EXTRA) for n in range(2)]
        bstage = ring[0:3 * E, 12288:15360]
        gfin = area[:, 13312:14336]
        iot = sb("iota_tables", [P, 512])
        i_blk1, i_slot1, i_exp = iot[:, 0:64], iot[:, 64:192], iot[:, 192:224]
        i_ext, i_tok, i_pmod, i_tok4 = iot[:, 224:240], iot[:, 240:244], iot[:, 244:245], iot[:, 248:252]
        i_reset, i_hi64, i_half = iot[:, 256:384], iot[:, 384:512], iot[:, 252:253]
        block_tab = sb("block_tables", [P, 3, 64])
        b_neg, b_mult, b_half = (block_tab[:, n, :] for n in range(3))
        st = sb("statistics", [P, 256])
        v8 = st[:, 0:32].rearrange("p (a m) -> p a m", a=NT)
        ngt, ssum, rinv = st[:, 32:36], st[:, 36:40], st[:, 40:44]
        ssq, rs = st[:, 44:48], st[:, 48:52]
        nx_f, far = st[:, 52:53], st[:, 53:54]
        idxf = st[:, 54:56]
        brt = st[0:E, 61:62]
        idx4 = st[:, 244:248]
        slotn, gcur = st[:, 56:60], st[:, 60:61]
        gate1, gate0 = st[:, 62:63], st[:, 63:64]
        cnt, nbx, exst = st[:, 64:96], st[:, 96:128], st[:, 128:160]
        bexp = st[:, 160:224]
        r1 = st[:, 224:228]
        slotd = st[:, 228:244].rearrange("p (a m) -> p a m", a=NT)
        rown = sb("rows_next", [P, 2], I32)
        row1, row0 = (sb(f"row_of_y{n}", [P, 1], I32) for n in (1, 0))
        rowc = sb("row_now", [P, 1], I32)
        ints = sb("block_ints", [P, 96], I32)
        bsel = sb("bias_selector", [3 * E, P], BF16)

        ld_x = [sem(f"x_loaded{a}") for a in range(NT)]
        ld_y = [sem(f"y_loaded{a}") for a in range(NT)]
        (ld_par, ld_mask, ld_pack, ld_wout, ld_xr, ld_wr, ld_bias, ld_gf, out_stored) = (sem(n) for n in (
            "params_loaded", "mask_loaded", "head_tables_loaded", "w_out_loaded", "x_reloaded", "w_router_loaded",
            "bias_loaded", "g_final_loaded", "out_stored"))
        ld_w = [sem(f"w_in_loaded{b}") for b in range(4)]
        w_used = [sem(f"w_in_used{b}") for b in range(4)]
        full = [sem(f"bank_full{b}") for b in range(8)]
        free = [sem(f"bank_free{b}") for b in range(8)]
        (init_done, root_done, h_ready, hT_ready, p_ready, q_ready, lora_in, sig_ready, a_ready,
         kr_ready, kksq_ready, kkroot_ready, rk_ready, cx_ready, kmod_ready, e1_free,
         e_ready, cm_ready) = (sem(n) for n in (
            "tables_set", "root_ready", "h_ready", "hT_ready", "projection_ready", "shifted_ready",
            "lora_inputs_ready", "decay_sigmoid_ready", "rate_ready", "kr_ready", "kk_squares_ready",
            "kk_root_ready", "bonus_products_ready", "log_decay_before_ready",
            "k_modified", "e1_place_free", "decay_exps_ready", "tilde_ready"))
        (conv_y, conv_root, conv_rec, conv_inv, gninv_ready, conv_done, tm_ready, l_ready, m_ready, t_ready,
         u_ready, x_ready, lb_ready,
         mv_ready, u0_ready, wt_ready, sa_ready, st_ready, pcm_ready, o_ready, centred, gnsq_ready, gnroot_ready,
         y_ready) = (sem(n) for n in (
            "conv_y", "conv_root", "conv_inverse", "conv_inverse_spread", "gn_inverse_ready", "conv_done",
            "time_major_ready", "L_ready", "MQ_ready",
            "T_ready", "U_ready", "X_ready", "level_ready", "mv_ready", "u0_ready", "wt_ready", "sa_ready",
            "state_ready", "chunk_decay_ready", "scan_output_ready", "centred", "gn_squares_ready",
            "gn_root_ready", "mixer_ready"))
        (x2_ready, root2_done, h2_ready, h2_stored, h2T_ready, lgT_ready, shift_ready,
         exp_ready, sel_ready, routed, extra_known, bias_ready, sum_ready, root3_done, fin_ready, moe_done) = (
            sem(n) for n in (
            "x2_ready", "root2_ready", "h2_ready", "h2_stored", "h2T_ready", "logitsT_ready",
            "gate_shift_ready", "gate_exps_ready", "selection_ready", "routed", "extra_blocks_known", "bias_ready",
            "sum_ready", "root3_ready", "final_ready", "experts_done"))
        gu_in = [sem(f"w_gu_in{k}") for k in range(KD)]
        gu_used = [sem(f"w_gu_used{k}") for k in range(KD)]
        dn_in = [sem(f"w_down_in{k}") for k in range(KD)]
        dn_used = [sem(f"w_down_used{k}") for k in range(KD - 1)]
        (s_sel, s_idx, s_row, s_bsel, s_cur, s_gath, s_scat, s_xt, s_xti, s_dn, s_y) = (sem(n) for n in (
            "slots_selected", "slot_index_out", "slot_rows_ready", "bias_selected", "slot_data_current",
            "gathered", "scattered", "x_transposed", "xinT_ready", "down_done", "y_ready"))
        s_gm, s_sg, s_at, s_ate = ([sem(f"{n}{h}") for h in range(2)] for n in (
            "gate_min_ready", "sigmoid_ready", "act_transposed", "actT_ready"))
        pool_turns = sem("pool_turns")
        s_gu = [sem(f"gate_up_done{h}") for h in range(2)]
        s_act = [sem(f"act_ready{h}") for h in range(2)]

        fills = {}
        per_bank = [0] * 8

        def plan(name, b):
            per_bank[b] += 1
            fills[name] = (b, per_bank[b])

        CONV_SUM_AT = 2
        LORA_AT, NORM_AT = 8, 10
        NLEV = len(LEVELS)
        for k in range(KD):
            plan(("hT", k), k)

        CONV_SPREAD = {1: (0, 1), 2: (2, 3)}

        def conv_spread(cp, lev):
            return CONV_SPREAD.get(lev, ()) if cp == NCP - 1 else ()

        def after_x2(a):
            return {2: (0,), 3: (1, 2, 3)}.get(a, ())

        for g in range(NG):
            for at_g, kinds in ((LORA_AT, ("w", "a")), (NORM_AT, ("kk", "bonus"))):
                for kind in kinds if g == at_g else ():
                    for j in range(NJ):
                        plan((kind, j), 4 + j)
            for q in range(g * GQ, (g + 1) * GQ):
                plan(("p", q), q % 4)
        for cp in range(NCP):
            for n in range(4):
                plan(("tm", cp, n), n)
            for name, b in (("L1", 4), ("LT", 6), ("MT", 0), ("QB", 2), ("QK", 4)):
                for par in range(2):
                    plan((name, cp, par), b + par)
            if cp > 0:
                plan(("mean", cp - 1), 0)
            for lev in range(NLEV):
                for par in range(2):
                    plan(("X", cp, lev, par), 6 + par)
                for par in range(2):
                    plan(("U", cp, lev, par), 2 + par)
                if cp > 0 and lev == 0:
                    plan(("var", cp - 1), 5)
                if cp > 0 and lev == 3:
                    plan(("spread", cp - 1), 0)
                for j in conv_spread(cp, lev):
                    plan(("conv_spread", j), 4 + j % 2)
            plan(("mv", cp), 4)
            plan(("u0", cp), 5)
            plan(("wt", cp), 6)
            plan(("o", cp), 4)
            for c in (2 * cp, 2 * cp + 1):
                plan(("sa", c), 7)
                if c < NCH - 1:
                    plan(("st", c), c % 2)
            if cp == CONV_SUM_AT:
                plan(("conv",), 6)
            if cp > 0:
                plan(("g", cp - 1), 5)
        last_cp = NCP - 1
        X2_BANK = {0: 6, 1: 0, 2: 2, 3: 6}
        H2_BANK = {0: 4, 1: 0, 2: 4, 3: 2}
        for name, b in ((("mean", last_cp), 4), (("x2", 0, 0), 6), (("var", last_cp), 5), (("x2", 0, 1), 7),
                        (("g", last_cp), 4), (("spread", last_cp), 5)):
            plan(name, b)
        for a in range(NT):
            if a > 0:
                for n in range(2):
                    plan(("x2", a, n), X2_BANK[a] + n)
            if a > 1:
                for m in after_x2(a):
                    for n in range(2):
                        plan(("h2T", m, n), H2_BANK[m] + n)
                    plan(("lgT", m), H2_BANK[m])
        for b, name in ((6, "lg"), (7, "rank"), (0, "cnt")):
            plan((name,), b)

        def fill(name):
            b, n = fills[name]
            if n > 1:
                nc.tensor.wait_ge(free[b], n - 1)
            return b

        def filled(eng, name):
            b, n = fills[name]
            eng.wait_ge(full[b], n)
            return b

        def slot(h):
            return (h % 2) * 4 + h // 2

        def flat(t):
            return t.rearrange("p a e -> p (a e)")

        block = ctx.enter_context(nc.Block())

        @block.sync
        def _(sp):
            xv = x.rearrange("(a p) n -> p a n", p=P)
            for a in range(NT):
                sp.dma_start(xa[:, a, :], xv[:, a, :]).then_inc(ld_x[a], 16)
            for dst, src in ((mats[:, 0:M_PACK, :], consts[:, 0:M_PACK, :]), (pc[:, :], pcol), (iot[:, :], iota[:, 0:512]),
                             (wup[:, 0, :], wa_up), (wup[:, 1, :], g_up), (brt, b_router)):
                sp.dma_start(dst, src).then_inc(ld_par, 16)
            for g in range(NG):
                b = g % 4
                if g >= 4:
                    sp.wait_ge(w_used[b], g // 4)
                sp.dma_start(wbuf[b], w_in[g]).then_inc(ld_w[b], 16)
                if g == 3:
                    sp.dma_start(rmask, iota[:, 512:1024]).then_inc(ld_mask, 16)
                    sp.dma_start(mats[:, M_PACK:M_N, :], consts[:, M_PACK:M_N, :]).then_inc(ld_pack, 16)
                    sp.dma_start(wout_sb, w_out.rearrange("(k p) n -> p k n", p=P)).then_inc(ld_wout, 16)
            sp.wait_ge(m_ready, NCP)
            for a in range(NT):
                sp.dma_start(xr[:, a, :], xv[:, a, :]).then_inc(ld_xr, 16)
            sp.wait_ge(o_ready, NCP)
            sp.wait_ge(conv_done, NJ)
            for n in range(3):
                sp.dma_start(bstage[n * E:(n + 1) * E, 0:2 * FF], b_gu).then_inc(ld_bias, 16)
                sp.dma_start(bstage[n * E:(n + 1) * E, 2 * FF:2 * FF + D], b_down).then_inc(ld_bias, 16)
            sp.dma_start(wr_sb, w_router.rearrange("(k p) e -> p k e", p=P)).then_inc(ld_wr, 16)

            def gu_rows(e, k):
                return w_gu[bass.ds(e * D + k * P, P), :]

            def down_rows(e, k):
                return w_down[bass.ds(e * FF + k * P, P), :]

            for k in range(6):
                sp.dma_start(wgu_sb[:, k, :], gu_rows(0, k)).then_inc(gu_in[k], 16)
            for a in range(NT):
                sp.wait_ge(h2_ready, a + 1)
                sp.dma_start(h2_dram[a * P:(a + 1) * P, :], h2[:, a, :]).then_inc(h2_stored, 16)
            for k in range(KD):
                sp.dma_start(wdn_sb[:, k, :], down_rows(0, k)).then_inc(dn_in[k], 16)
            sp.wait_ge(bias_ready, 1)
            for k in (6, 7):
                sp.dma_start(wgu_sb[:, k, :], gu_rows(0, k)).then_inc(gu_in[k], 16)

            def expert_weights(i, e):
                for k in range(KD):
                    sp.wait_ge(gu_used[k], i)
                    sp.dma_start(wgu_sb[:, k, :], gu_rows(e, k)).then_inc(gu_in[k], 16)
                for k in range(KD):
                    if k < KD - 1:
                        sp.wait_ge(dn_used[k], i)
                    else:
                        sp.wait_ge(s_dn, i + 1)
                    sp.dma_start(wdn_sb[:, k, :], down_rows(e, k)).then_inc(dn_in[k], 16)

            with sp.Fori(1, E) as i:
                expert_weights(i, i)
            sp.wait_ge(routed, 1)
            sp.wait_ge(extra_known, 1)
            n_extra = sp.value_load(ints[0:1, EXTRA:EXTRA + 1], min_val=0, max_val=EXTRA - 1)
            with sp.If(n_extra > 0):
                with sp.Fori(0, n_extra) as j:
                    e = sp.value_load(ints[0:1, bass.ds(j, 1)], min_val=0, max_val=E - 1)
                    expert_weights(j + E, e)
            sp.wait_ge(h2_stored, 16 * NT)
            sp.dma_start(gfin, g_final.to_broadcast((P, D))).then_inc(ld_gf, 16)
            sp.wait_ge(moe_done, 1)
            yv = y_dram.rearrange("(a p k) n -> p a (k n)", p=P, k=TOPK)
            for a in range(NT):
                sp.dma_start(ring[:, a * 4096:(a + 1) * 4096], yv[:, a, :]).then_inc(ld_y[a], 16)
            ov = out.rearrange("(a p) n -> p a n", p=P)
            for a in range(NT):
                sp.wait_ge(fin_ready, a + 1)
                sp.dma_start(ov[:, a, :], xr[:, a, :]).then_inc(out_stored, 16)
            sp.wait_ge(out_stored, 16 * NT)

        @block.gpsimd
        def _(pool):
            pool.wait_ge(w_used[0], 4)
            for b in range(1, 4):
                pool.wait_ge(w_used[b], 3)
            pool.memset(state[0], 0.0)
            pool.memset(sa, 0.0)
            pool.drain().then_inc(init_done, 1)

            def conv(j):
                u, bg, z = pT[:, Q_U + j, :], pT[:, Q_B + j, :], pT[:, Q_C + j, :]
                pool.drain()
                pool.tensor_tensor(z, z, u, ALU.mult)
                pool.drain()
                pool.tensor_scalar(u, z, pc[:, PC_CW + 8 + j:PC_CW + 9 + j], None, ALU.mult)
                for lag, row_w in ((1, 4), (2, 0)):
                    w = pc[:, PC_CW + row_w + j:PC_CW + row_w + j + 1]
                    pool.drain()
                    pool.tensor_scalar(conv_t, z, w, None, ALU.mult)
                    pool.drain()
                    pool.tensor_tensor(u[:, lag:], u[:, lag:], conv_t[:, :T - lag], ALU.add)
                pool.drain()
                pool.tensor_tensor(u, u, bg, ALU.mult)
                pool.drain()
                pool.tensor_tensor(z, u, u, ALU.mult).then_inc(conv_y, 1)

            def conv_norm(j):
                pool.wait_ge(conv_inv, j + 1)
                u, z = pT[:, Q_U + j, :], pT[:, Q_C + j, :]
                pool.drain()
                pool.tensor_tensor(u, u, z, ALU.mult)
                pool.drain()
                pool.tensor_scalar(u, u, pc[:, PC_CG + j:PC_CG + j + 1], None, ALU.mult)
                pool.drain().then_inc(conv_done, 1)

            pool.wait_ge(ld_par, 96)
            pool.wait_ge(p_ready, NQ)
            pool.wait_ge(cm_ready, 1)
            for cp in range(NCP):
                for lev in range(NLEV):
                    if lev == 0:
                        pool.wait_ge(l_ready, cp + 1)
                    else:
                        filled(pool, ("X", cp, lev - 1, 1))
                    m = mats[:, M_LEV + lev:M_LEV + lev + 1, :].to_broadcast((P, NH, P))
                    pool.tensor_tensor(LB, LL, m, ALU.mult).then_inc(lb_ready, 1)
                    if lev < 2 and 2 * cp + lev < NCH - 1:
                        c = 2 * cp + lev
                        if c >= 2:
                            pool.wait_ge(st_ready, c - 1)
                        pool.tensor_tensor(pcm[c % 2], head_ones.rearrange("p (o v) -> p o v", o=1).to_broadcast((P, NJ, P)),
                                           pend[:, :, c:c + 1].to_broadcast((P, NJ, P)), ALU.mult).then_inc(pcm_ready, 1)
                if cp < 2:
                    for j in (2 * cp, 2 * cp + 1):
                        conv(j)
                if cp == NCP - 1:
                    for j in range(NJ):
                        conv_norm(j)
            pool.wait_ge(ld_bias, 96)
            pool.drain()
            pool.tensor_copy(bparts, bstage)
            for rnd in (1, 2):
                pool.drain()
                pool.tensor_tensor(bstage, bstage, bparts, ALU.subtract)
                for n in range(rnd, 3):
                    rows = slice(n * E, (n + 1) * E)
                    pool.drain()
                    last = pool.tensor_copy(bparts[rows, :], bstage[rows, :])
            last.then_inc(bias_ready, 1)

            def small(i):
                return pool.value_load(ints[0:1, bass.ds(i + 32, 1)], min_val=0, max_val=1)

            def gather(halves):
                src = h2_dram.rearrange("t (f n) -> (t f) n", f=2) if halves else h2_dram
                pool.indirect_dma_start(xg[:, 0:D // 2] if halves else xg, None, src,
                                        bass.IndirectOffsetOnAxis(ap=rown[:, 0:1], axis=0),
                                        bounds_check=src.shape[0] - 1, oob_is_err=False).then_inc(s_gath, 16)

            def scatter(halves):
                dst = y_dram.rearrange("t (f n) -> (t f) n", f=2) if halves else y_dram
                pool.indirect_dma_start(dst, bass.IndirectOffsetOnAxis(ap=rowc[:, 0:1], axis=0),
                                        yb[:, 0:D // 2] if halves else yb, None,
                                        bounds_check=dst.shape[0] - 1, oob_is_err=False).then_inc(s_scat, 16)

            def pool_block(i):
                pool.wait_ge(s_row, i + 3)
                pool.wait_ge(s_xt, i + 2)
                pool.sem_inc(pool_turns, 1)
                with pool.If(small(i + 2) > 0):
                    gather(True)
                with pool.Else():
                    gather(False)
                pool.wait_ge(s_y, i + 2)
                pool.sem_inc(pool_turns, 1)
                with pool.If(small(i) > 0):
                    scatter(True)
                with pool.Else():
                    scatter(False)

            pool.wait_ge(lgT_ready, NT)
            pool.drain()
            pool.memset(xg, 0.0)
            pool.memset(yb, 0.0)
            pool.memset(rowc[:, :], int(FAR))
            pool.drain()
            scatter(False)
            pool.wait_ge(h2_stored, 16 * NT)
            pool.wait_ge(routed, 1)
            for b in range(2):
                pool.wait_ge(s_row, b + 1)
                if b:
                    pool.wait_ge(s_xt, b)
                with pool.If(small(b) > 0):
                    gather(True)
                with pool.Else():
                    gather(False)
            n_extra = pool.value_load(ints[0:1, EXTRA:EXTRA + 1], min_val=0, max_val=EXTRA - 1)
            with pool.Fori(0, E) as i:
                pool_block(i)
            with pool.If(n_extra > 0):
                with pool.Fori(0, n_extra) as j:
                    pool_block(j + E)
            pool.wait_ge(s_scat, (n_extra + E) * 16 + 16)
            pool.wait_ge(s_gath, (n_extra + E) * 16 + 32)
            pool.sem_inc(moe_done, 1)

        @block.scalar
        def _(act):
            def col(n):
                return pc[:, n:n + 1]

            act.sem_inc(s_y, 1)
            act.wait_ge(init_done, 1)
            for a in range(NT):
                act.wait_ge(ld_x[a], 16)
                nc.scalar.activation(x_sq[:, a, :], xa[:, a, :], ACT.Square, accum_out=ssq[:, a:a + 1])
                act.drain()
                nc.scalar.activation(rs[:, a:a + 1], ssq[:, a:a + 1], ACT.Sqrt, scale=1.0 / D,
                                     bias=eps_c).then_inc(root_done, 1)
            act.wait_ge(ld_par, 96)
            for k in range(1, KD, 2):
                b = filled(act, ("hT", k))
                nc.scalar.activation(hT[:, k, :], bank(b), ACT.Copy, scale=col(PC_GMIX + k)).then_inc(free[b], 1)

            def evacuate_p(q):
                b = filled(act, ("p", q))
                nc.scalar.activation(pT[:, q, :], bank(b), ACT.Copy).then_inc(free[b], 1)
                act.drain().then_inc(p_ready, 1)

            act.wait_ge(root_done, NT)
            for q in range(Q_G + 2):
                evacuate_p(q)
            act.wait_ge(q_ready, 14)
            nc.scalar.activation(pT[0:64, Q_WA, :], pT[0:64, Q_WA, :], ACT.Tanh)
            nc.scalar.activation(pT[:, Q_G, :], pT[:, Q_G, :], ACT.Sigmoid).then_inc(lora_in, 1)
            for q in range(Q_G + 2, GQ * LORA_AT):
                evacuate_p(q)
            for kind, dst, bias_at, done in (("w", ldec, PC_W0, sig_ready), ("a", bt, PC_A0, a_ready)):
                for j in range(NJ):
                    b = filled(act, (kind, j))
                    nc.scalar.activation(dst[:, j, :], bank(b), ACT.Sigmoid, bias=col(bias_at + j)).then_inc(free[b], 1)
                act.drain().then_inc(done, 1)
            act.wait_ge(kr_ready, 1)
            nc.scalar.activation(dbuf, at, ACT.Square).then_inc(kksq_ready, 1)
            for q in range(GQ * LORA_AT, GQ * NORM_AT):
                evacuate_p(q)
                if q == GQ * LORA_AT + 1:
                    act.wait_ge(cx_ready, 1)
                    nc.scalar.activation(ldec, ldec, ACT.Exp)
            for j in range(NJ):
                b = filled(act, ("kk", j))
                nc.scalar.activation(dbuf[:, j, :], bank(b), ACT.Sqrt).then_inc(free[b], 1)
            act.drain().then_inc(kkroot_ready, 1)
            act.wait_ge(kmod_ready, 1)
            nc.scalar.activation(e2, cdec, ACT.Exp, scale=-1.0)
            for q in range(GQ * NORM_AT, NQ):
                evacuate_p(q)
                if q == NQ - 3:
                    act.wait_ge(e1_free, 1)
                    nc.scalar.activation(dbuf, cdec, ACT.Exp).then_inc(e_ready, 1)

            def cols3(t, cp):
                return t[:, :, cp * P:(cp + 1) * P]

            def bank3(b):
                return bank(b).rearrange("p (j t) -> p j t", j=NJ)

            def scan_squares(cp):
                act.wait_ge(centred, cp + 1)
                nc.scalar.activation(cols3(tmpo, cp), cols3(oT, cp), ACT.Square).then_inc(gnsq_ready, 1)

            def scan_root(cp):
                b = filled(act, ("var", cp))
                nc.scalar.activation(scan_rms[:, cp * P:(cp + 1) * P], bank(b, 0, P), ACT.Sqrt, scale=1.0 / 64,
                                     bias=gneps_c).then_inc(free[b], 1)
                act.drain().then_inc(gnroot_ready, 1)

            for cp in range(NCP):
                for n, dst in ((2, ktm), (3, vtm)):
                    b = filled(act, ("tm", cp, n))
                    nc.scalar.activation(dst, bank(b), ACT.Copy).then_inc(free[b], 1)
                act.drain().then_inc(tm_ready, 2)
                for par in range(2):
                    b = filled(act, ("L1", cp, par))
                    nc.scalar.activation(LL[:, par * 4:par * 4 + 4, :], bank3(b), ACT.Copy).then_inc(free[b], 1)
                act.drain().then_inc(l_ready, 1)
                for lev in range(NLEV):
                    for par in range(2):
                        b = filled(act, ("X", cp, lev, par))
                        nc.scalar.activation(XI[:, par * 4:par * 4 + 4, :], bank3(b), ACT.Copy).then_inc(free[b], 1)
                        act.drain().then_inc(x_ready, 1)
                    if cp > 0 and lev == 0:
                        scan_squares(cp - 1)
                    if cp > 0 and lev == 1:
                        scan_root(cp - 1)
                    for j in conv_spread(cp, lev):
                        b = filled(act, ("conv_spread", j))
                        nc.scalar.activation(pT[:, Q_C + j, :], bank(b), ACT.Copy).then_inc(free[b], 1)
                        act.drain().then_inc(conv_inv, 1)
                for name, dst, done in (("mv", mv, mv_ready), ("wt", wt, wt_ready), ("u0", u0, u0_ready)):
                    b = filled(act, (name, cp))
                    nc.scalar.activation(dst, bank(b), ACT.Copy).then_inc(free[b], 1)
                    act.drain().then_inc(done, 1)
                if cp == CONV_SUM_AT:
                    b = filled(act, ("conv",))
                    nc.scalar.activation(conv_rms, bank(b), ACT.Sqrt, scale=1.0 / 64, bias=eps_c).then_inc(free[b], 1)
                    act.drain().then_inc(conv_root, 1)
                b = filled(act, ("o", cp))
                nc.scalar.activation(cols3(oT, cp), bank3(b), ACT.Copy).then_inc(free[b], 1)
                act.drain().then_inc(o_ready, 1)
            scan_squares(last_cp)
            scan_root(last_cp)
            for a in range(NT):
                act.wait_ge(x2_ready, a + 1)
                nc.scalar.activation(h2[:, a, :], xr[:, a, :], ACT.Square, accum_out=ssq[:, a:a + 1])
                act.drain()
                nc.scalar.activation(rs[:, a:a + 1], ssq[:, a:a + 1], ACT.Sqrt, scale=1.0 / D,
                                     bias=eps_c).then_inc(root2_done, 1)
            act.wait_ge(shift_ready, 1)
            nc.scalar.activation(gate, t_b, ACT.Exp).then_inc(exp_ready, 1)

            def sigmoid(i, h):
                act.wait_ge(s_gm[h], i + 1)
                act.wait_ge(s_act[h], i + 1)
                return nc.scalar.activation(sg[:, h, :], gm[:, h, :], ACT.Sigmoid, scale=1.702)

            def act_block(i):
                small = act.value_load(ints[0:1, bass.ds(i + 32, 1)], min_val=0, max_val=1)
                with act.If(small > 0):
                    sigmoid(i, 0).then_inc(s_sg[0], 1)
                    act.wait_ge(s_at[0], i + 1)
                    nc.scalar.activation(actT.rearrange("p (f k) s -> p k f s", f=2)[:, :, :, 0:HALF],
                                         bank(0).rearrange("p (k f s) -> p k f s", f=2, s=HALF),
                                         ACT.Copy).then_inc(s_ate[0], 1)
                    act.drain().then_inc(s_sg[1], 1)
                    act.drain().then_inc(s_ate[1], 1)
                    act.wait_ge(s_dn, i + 2)
                    act.wait_ge(s_cur, i + 1)
                    act.wait_ge(s_scat, 16 * i + 16)
                    nc.scalar.activation(yb[:, 0:512], bank(4), ACT.Copy, scale=gcur).then_inc(s_y, 1)
                with act.Else():
                    for h in range(2):
                        sigmoid(i, h).then_inc(s_sg[h], 1)
                    for h in range(2):
                        act.wait_ge(s_at[h], i + 1)
                        nc.scalar.activation(actT[:, 4 * h:4 * h + 4, :], bank(2 * h).rearrange("p (k s) -> p k s", k=4),
                                             ACT.Copy).then_inc(s_ate[h], 1)
                    act.wait_ge(s_dn, i + 2)
                    act.wait_ge(s_cur, i + 1)
                    act.wait_ge(s_scat, 16 * i + 16)
                    nc.scalar.activation(yb, psum[:, 4 * 512:6 * 512], ACT.Copy, scale=gcur).then_inc(s_y, 1)

            act.wait_ge(routed, 1)
            n_extra = act.value_load(ints[0:1, EXTRA:EXTRA + 1], min_val=0, max_val=EXTRA - 1)
            with act.Fori(0, E) as i:
                act_block(i)
            with act.If(n_extra > 0):
                with act.Fori(0, n_extra) as j:
                    act_block(j + E)
            for a in range(NT):
                act.wait_ge(sum_ready, a + 1)
                nc.scalar.activation(area[:, 8192 + a * 1024:9216 + a * 1024], xr[:, a, :], ACT.Square,
                                     accum_out=ssq[:, a:a + 1])
                act.drain()
                nc.scalar.activation(rs[:, a:a + 1], ssq[:, a:a + 1], ACT.Sqrt, scale=1.0 / D,
                                     bias=eps_c).then_inc(root3_done, 1)

        @block.vector
        def _(dve):
            def col(n):
                return pc[:, n:n + 1]

            def tt(out, a, b, op):
                return nc.vector.tensor_tensor(out, a, b, op)

            def ts(out, a, s1, s2, op0, op1=None):
                if op1 is None:
                    return nc.vector.tensor_scalar(out, a, s1, None, op0)
                return nc.vector.tensor_scalar(out, a, s1, s2, op0, op1)

            def stt(out, a, s, b, op0, op1):
                return nc.vector.scalar_tensor_tensor(out=out, in0=a, scalar=s, in1=b, op0=op0, op1=op1)

            for h in range(2):
                dve.sem_inc(s_act[h], 1)
            nc.vector.memset(eps_c, EPS)
            nc.vector.memset(gneps_c, GN_EPS)
            dve.drain().then_inc(init_done, 1)
            for a in range(NT):
                dve.wait_ge(root_done, a + 1)
                nc.vector.reciprocal(rs[:, a:a + 1], rs[:, a:a + 1])
                dve.drain()
                ts(xa[:, a, :], xa[:, a, :], rs[:, a:a + 1], None, ALU.mult).then_inc(h_ready, 1)
            dve.wait_ge(ld_par, 96)
            for k in range(0, KD, 2):
                b = filled(dve, ("hT", k))
                ts(hT[:, k, :], bank(b), col(PC_GMIX + k), None, ALU.mult).then_inc(free[b], 1)
            dve.drain().then_inc(hT_ready, 1)
            for q0, n in ((Q_R, 4), (Q_K, 4), (Q_V, 4), (Q_WA, 2)):
                dve.wait_ge(p_ready, q0 + n)
                pq = pT[:, q0:q0 + n, :]
                tt(dbuf[:, 0:n, 1:], pq[:, :, :T - 1], pq[:, :, 1:], ALU.subtract)
                ts(dbuf[:, 0:n, 0:1], pq[:, :, 0:1], -1.0, None, ALU.mult)
                dve.drain()
                for m in range(n):
                    stt(pq[:, m, :], dbuf[:, m, :], col(PC_MU + q0 + m), pq[:, m, :], ALU.mult,
                        ALU.add).then_inc(q_ready, 1)
                dve.drain()
            for j in range(NJ):
                ts(at[:, j, :], pT[:, Q_K + j, :], col(PC_KK + j), None, ALU.mult)
            dve.drain().then_inc(kr_ready, 1)
            dve.wait_ge(sig_ready, 1)
            ts(ldec, ldec, DECAY_SCALE, None, ALU.mult)
            dve.drain()
            dve.wait_ge(ld_mask, 16)
            for j in range(NJ):
                nc.vector.tensor_tensor_scan(cdec[:, j, :], rmask, ldec[:, j, :], 0.0, ALU.mult, ALU.add)
            dve.drain()
            tt(ldec, cdec, ldec, ALU.subtract).then_inc(cx_ready, 1)
            dve.wait_ge(a_ready, 1)
            for j in range(NJ):
                ts(e2[:, j, :], bt[:, j, :], 1.0, col(PC_KA + j), ALU.subtract, ALU.mult)
            dve.drain()
            for j in range(NJ):
                kj = pT[:, Q_K + j, :]
                stt(kj, e2[:, j, :], 1.0, kj, ALU.add, ALU.mult)
            dve.drain().then_inc(kmod_ready, 1)
            for j in range(NJ):
                stt(bonus[:, j, :], pT[:, Q_R + j, :], col(PC_RK + j), pT[:, Q_K + j, :], ALU.mult, ALU.mult)
            dve.drain().then_inc(rk_ready, 1)
            dve.wait_ge(kkroot_ready, 1)
            ts(dbuf, dbuf, 1e-12, None, ALU.max)
            dve.drain()
            nc.vector.reciprocal(dbuf, dbuf)
            dve.drain()
            tt(at, at, dbuf, ALU.mult)
            dve.drain().then_inc(e1_free, 1)
            stt(bt, at, -1.0, bt, ALU.mult, ALU.mult)
            for j in range(NJ):
                b = filled(dve, ("bonus", j))
                tt(bonus[:, j, :], bank(b), pT[:, Q_V + j, :], ALU.mult).then_inc(free[b], 1)
            dve.wait_ge(e_ready, 1)
            dve.drain()
            tt(bt, bt, e2, ALU.mult)
            tt(at, at, ldec, ALU.mult)
            tt(pT[:, Q_K:Q_K + 4, :], pT[:, Q_K:Q_K + 4, :], e2, ALU.mult)
            tt(pT[:, Q_R:Q_R + 4, :], pT[:, Q_R:Q_R + 4, :], dbuf, ALU.mult)
            nc.vector.tensor_copy(pend, dbuf.rearrange("p j (c t) -> p j c t", c=NCH)[:, :, :, C - 1])
            dve.drain().then_inc(cm_ready, 1)

            def cols3(t, cp):
                return t[:, :, cp * P:(cp + 1) * P]

            def bank3(b):
                return bank(b).rearrange("p (j t) -> p j t", j=NJ)

            def per_channel(n):
                return pc[:, n:n + NJ].rearrange("p (j o) -> p j o", o=1).to_broadcast((P, NJ, P))

            def scan_centre(cp):
                b = filled(dve, ("mean", cp))
                dve.wait_ge(o_ready, cp + 1)
                stt(cols3(oT, cp), bank3(b), -1.0 / 64, cols3(oT, cp), ALU.mult, ALU.add).then_inc(free[b], 1)
                dve.drain().then_inc(centred, 1)

            def scan_inverse(cp):
                dve.wait_ge(gnroot_ready, cp + 1)
                z = scan_rms[:, cp * P:(cp + 1) * P]
                nc.vector.reciprocal(z, z)
                dve.drain().then_inc(gninv_ready, 1)

            def scan_unit(cp):
                b = filled(dve, ("spread", cp))
                tt(cols3(oT, cp), cols3(oT, cp), bank3(b), ALU.mult).then_inc(free[b], 1)
                dve.drain()

            def scan_gate(cp):
                o = cols3(oT, cp)
                tt(o, o, per_channel(PC_GNW), ALU.mult)
                dve.drain()
                tt(o, o, per_channel(PC_GNB), ALU.add)
                dve.drain()
                tt(o, o, cols3(bonus, cp), ALU.add)
                dve.drain()
                b = filled(dve, ("g", cp))
                tt(cols3(pT[:, Q_R:Q_R + NJ, :], cp), bank3(b), o, ALU.mult).then_inc(free[b], 1)
                dve.drain().then_inc(y_ready, 1)

            def masked(dst, b, m):
                return tt(dst, bank(b).rearrange("p (s t) -> p s t", s=4),
                          mats[:, m:m + 1, :].to_broadcast((P, 4, P)), ALU.mult)

            ident8 = mats[:, M_ID:M_ID + 1, :].to_broadcast((P, NH, P))

            def transposed(hs):
                return nc.vector.transpose(TI[:, hs, :].rearrange("p s t -> p (s t)"),
                                           UI[:, hs, :].rearrange("p s t -> p (s t)"))

            for cp in range(NCP):
                for n, dst in ((0, atm), (1, btm)):
                    b = filled(dve, ("tm", cp, n))
                    nc.vector.tensor_copy(dst, bank(b)).then_inc(free[b], 1)
                dve.drain().then_inc(tm_ready, 2)
                for par in range(2):
                    b = filled(dve, ("LT", cp, par))
                    masked(UI[:, par * 4:par * 4 + 4, :], b, M_L1UP).then_inc(free[b], 1)
                dve.drain()
                tt(UI, UI, ident8, ALU.add)
                dve.drain().then_inc(u_ready, 2)
                transposed(slice(0, NH))
                dve.drain().then_inc(t_ready, 2)
                for name, dst, m in (("MT", MT, M_STRICT), ("QB", QB, M_INCL), ("QK", QK, M_INCL)):
                    for par in range(2):
                        b = filled(dve, (name, cp, par))
                        masked(dst[:, par * 4:par * 4 + 4, :], b, m).then_inc(free[b], 1)
                dve.drain().then_inc(m_ready, 1)
                if cp > 0:
                    scan_centre(cp - 1)
                for lev in range(NLEV):
                    for par in range(2):
                        hs = slice(par * 4, par * 4 + 4)
                        b = filled(dve, ("U", cp, lev, par))
                        tt(UI[:, hs, :], UI[:, hs, :], bank3(b), ALU.add).then_inc(free[b], 1)
                        dve.drain().then_inc(u_ready, 1)
                    if lev < NLEV - 1:
                        for par in range(2):
                            transposed(slice(par * 4, par * 4 + 4))
                            dve.drain().then_inc(t_ready, 1)
                    if cp > 0 and lev == 2:
                        scan_inverse(cp - 1)
                if cp > 0:
                    scan_unit(cp - 1)
                for c in (2 * cp, 2 * cp + 1):
                    rows = slice((c % 2) * C, (c % 2) * C + C)
                    b = filled(dve, ("sa", c))
                    dve.wait_ge(u0_ready, cp + 1)
                    tt(sa[rows, :], psum[rows, b * 512:(b + 1) * 512], u0[rows, :], ALU.add).then_inc(free[b], 1)
                    dve.drain().then_inc(sa_ready, 1)
                    if c == NCH - 1:
                        break
                    b = filled(dve, ("st", c))
                    tt(tmp_state, bank(b).rearrange("p (j v) -> p j v", j=NJ), state[c % 3], ALU.add).then_inc(free[b], 1)
                    dve.drain()
                    dve.wait_ge(pcm_ready, c + 1)
                    tt(state[(c + 1) % 3], tmp_state, pcm[c % 2], ALU.mult)
                    dve.drain().then_inc(st_ready, 1)
                if cp > 0:
                    scan_gate(cp - 1)
                if cp == CONV_SUM_AT:
                    dve.wait_ge(conv_root, 1)
                    nc.vector.reciprocal(conv_rms, conv_rms)
                    dve.drain().then_inc(conv_rec, 1)
            scan_centre(last_cp)
            scan_inverse(last_cp)
            scan_unit(last_cp)
            scan_gate(last_cp)
            dve.wait_ge(ld_xr, 16 * NT)
            dve.wait_ge(ld_par, 96)

            def residual(a):
                for n in range(2):
                    b = filled(dve, ("x2", a, n))
                    xs = xr[:, a, n * 512:(n + 1) * 512]
                    tt(xs, xs, bank(b), ALU.add).then_inc(free[b], 1)
                dve.drain().then_inc(x2_ready, 1)

            def second_norm(a):
                dve.wait_ge(root2_done, a + 1)
                nc.vector.reciprocal(rs[:, a:a + 1], rs[:, a:a + 1])
                dve.drain()
                ts(h2[:, a, :], xr[:, a, :], rs[:, a:a + 1], None, ALU.mult).then_inc(h2_ready, 1)

            def h2_gain(a):
                for n in range(2):
                    b = filled(dve, ("h2T", a, n))
                    tt(h2T[:, 4 * n:4 * n + 4, a * P:(a + 1) * P], bank3(b),
                       pc[:, PC_GFFN + 4 * n:PC_GFFN + 4 * n + 4].rearrange("p (k o) -> p k o", o=1)
                       .to_broadcast((P, 4, P)), ALU.mult).then_inc(free[b], 1)
                dve.drain().then_inc(h2T_ready, 1)

            def logits_bias(a):
                b = filled(dve, ("lgT", a))
                ts(lgts[:, a * P:(a + 1) * P], psum[0:E, b * 512:b * 512 + P], brt, None, ALU.add).then_inc(free[b], 1)
                dve.drain().then_inc(lgT_ready, 1)

            residual(0)
            second_norm(0)
            residual(1)
            second_norm(1)
            residual(2)
            second_norm(2)
            h2_gain(0)
            logits_bias(0)
            residual(3)
            h2_gain(1)
            second_norm(3)
            logits_bias(1)
            for a in (2, 3):
                h2_gain(a)
                logits_bias(a)
            b = filled(dve, ("lg",))
            nc.vector.tensor_copy(lg, bank(b, 0, NS).rearrange("p (a e) -> p a e", a=NT)).then_inc(free[b], 1)
            dve.drain()
            for a in range(NT):
                nc.vector.max(v8[:, a, :], lg[:, a, :])
            dve.drain()
            fourth = v8[:, :, 3:4].to_broadcast((P, NT, E))
            tt(t_a, lg, fourth, ALU.is_gt)
            tt(t_c, lg, fourth, ALU.is_equal)
            tt(t_b, lg, v8[:, :, 0:1].to_broadcast((P, NT, E)), ALU.subtract).then_inc(shift_ready, 1)
            dve.drain()
            nc.vector.reduce_sum(ngt, t_a, AX.X)
            nc.vector.tensor_tensor_scan(flat(t_d), i_reset, flat(t_c), 0.0, ALU.mult, ALU.add)
            dve.drain()
            tt(t_d, t_d, ngt.rearrange("p (a o) -> p a o", o=1).to_broadcast((P, NT, E)), ALU.add)
            dve.drain()
            ts(t_d, t_d, float(TOPK), None, ALU.is_le)
            dve.drain()
            tt(t_c, t_c, t_d, ALU.mult)
            dve.drain()
            tt(sel, t_a, t_c, ALU.add)
            dve.drain()
            nc.vector.tensor_copy(psel[:, 0, :], sel[:, 0, :])
            for a in range(1, NT):
                dve.drain()
                tt(psel[:, a, :], psel[:, a - 1, :], sel[:, a, :], ALU.add)
            dve.drain().then_inc(sel_ready, 1)
            dve.wait_ge(exp_ready, 1)
            tt(gate, gate, sel, ALU.mult)
            nc.vector.tensor_tensor_scan(flat(krank), i_reset, flat(sel), 0.0, ALU.mult, ALU.add)
            dve.drain()
            nc.vector.reduce_sum(ssum, gate, AX.X)
            tt(krank, krank, sel, ALU.subtract)
            dve.drain()
            nc.vector.reciprocal(rinv, ssum)
            dve.drain()
            tt(gate, gate, rinv.rearrange("p (a o) -> p a o", o=1).to_broadcast((P, NT, E)), ALU.mult)
            b = filled(dve, ("rank",))
            nc.vector.tensor_copy(rank, bank(b, 0, NS).rearrange("p (a e) -> p a e", a=NT)).then_inc(free[b], 1)
            b = filled(dve, ("cnt",))
            sums = bank(b, 0, NS).rearrange("p (a e) -> p a e", a=NT)
            dve.drain()
            tt(rank[:, 1:, :], rank[:, 1:, :], sums[:, 0:NT - 1, :], ALU.add)
            nc.vector.tensor_copy(cnt, sums[:, NT - 1, :]).then_inc(free[b], 1)
            dve.drain()
            nc.vector.memset(b_neg, 0.0)
            dve.drain()
            ts(b_neg[:, 0:E], cnt, float(HALF), -1.0, ALU.is_le, ALU.mult)
            dve.drain()
            ts(b_mult, b_neg, -1.0, 1.0, ALU.mult, ALU.add)
            ts(b_half, b_neg, i_half, -1.0, ALU.mult, ALU.mult)
            ts(t_a, rank, float(SLOTS), None, ALU.is_ge)
            ts(nbx, cnt, float(SLOTS), None, ALU.is_gt)
            for m in range(2, T // SLOTS):
                dve.drain()
                stt(t_a, rank, float(m * SLOTS), t_a, ALU.is_ge, ALU.add)
                stt(nbx, cnt, float(m * SLOTS), nbx, ALU.is_gt, ALU.add)
            dve.drain()
            stt(rmod1, t_a, -float(SLOTS), rank, ALU.mult, ALU.add)
            nc.vector.tensor_tensor_scan(exst, ones[:, 0:E], nbx, 0.0, ALU.mult, ALU.add)
            dve.drain()
            ts(rmod1, rmod1, 1.0, None, ALU.add)
            nc.vector.tensor_copy(nx_f, exst[:, E - 1:E])
            dve.drain()
            tt(exst, exst, nbx, ALU.subtract)
            dve.drain()
            ex4 = exst.rearrange("p (o e) -> p o e", o=1).to_broadcast((P, NT, E))
            e4 = i_exp.rearrange("p (o e) -> p o e", o=1).to_broadcast((P, NT, E))
            tt(t_b, t_a, ex4, ALU.add)
            ts(t_d, t_a, 1.0, None, ALU.is_ge)
            dve.drain()
            ts(t_b, t_b, float(E - 1), None, ALU.add)
            dve.drain()
            tt(t_b, t_b, e4, ALU.subtract)
            dve.drain()
            tt(t_b, t_b, t_d, ALU.mult)
            dve.drain()
            tt(t_b, t_b, e4, ALU.add)
            dve.drain()
            stt(blk1, t_b, 1.0, sel, ALU.add, ALU.mult)
            nc.vector.tensor_copy(ints[:, EXTRA:EXTRA + 1], nx_f)
            ts(ints[:, 32:96], b_neg, -1.0, None, ALU.mult)
            nc.vector.tensor_copy(slotd[:, :, 0], i_tok)
            nc.vector.memset(slotd[:, :, 3], 1.0)
            dve.drain().then_inc(routed, 1)

            def select_slots(b):
                ts(t_a, blk1, i_blk1[:, b], None, ALU.is_equal)
                stt(slot_id, i_hi64, b_neg[:, b], i_slot1, ALU.mult, ALU.add)
                dve.drain()
                tt(t_b, t_a, rmod1, ALU.mult)
                tt(t_c, t_a, krank, ALU.mult)
                tt(t_d, t_a, gate, ALU.mult)
                dve.drain()
                nc.vector.reduce_sum(r1, t_b, AX.X)
                nc.vector.reduce_sum(idx4, t_c, AX.X)
                nc.vector.reduce_sum(slotd[:, :, 2], t_d, AX.X)
                dve.drain()
                tt(slotd[:, :, 1], idx4, i_tok4, ALU.add)
                for a in range(NT):
                    ts(sel4[:, a, :], slot_id, r1[:, a:a + 1], None, ALU.is_equal)
                dve.drain().then_inc(s_sel, 1)

            def slot_rows(b):
                nc.vector.tensor_copy(slotn, bank(6, 0, 4))
                dve.drain()
                ts(far, slotn[:, 3:4], -FAR, FAR, ALU.mult, ALU.add)
                dve.drain()
                ts(idxf, slotn[:, 0:2], far, None, ALU.add)
                dve.drain()
                ts(idxf, idxf, b_mult[:, b], b_half[:, b], ALU.mult, ALU.add)
                dve.drain()
                nc.vector.tensor_copy(rown[:, :], idxf)
                dve.drain().then_inc(s_row, 1)

            def small(i):
                return dve.value_load(ints[0:1, bass.ds(i + 32, 1)], min_val=0, max_val=1)

            def x_small():
                tt(xiT.rearrange("p (f k) s -> p k f s", f=2)[:, :, :, 0:HALF],
                   bank(7).rearrange("p (k f s) -> p k f s", f=2, s=HALF),
                   pc[:, PC_GFFN:PC_GFFN + KD].rearrange("p (f k o) -> p k f o", f=2, o=1)
                   .to_broadcast((P, 4, 2, HALF)), ALU.mult).then_inc(s_xti, 1)

            def x_large():
                for half in range(2):
                    last = tt(xiT[:, 4 * half:4 * half + 4, :], bank(7 - half).rearrange("p (k s) -> p k s", k=4),
                              pc[:, PC_GFFN + 4 * half:PC_GFFN + 4 * half + 4].rearrange("p (k o) -> p k o", o=1)
                              .to_broadcast((P, 4, P)), ALU.mult)
                last.then_inc(s_xti, 1)

            def swiglu(i, h):
                dve.wait_ge(s_gu[h], i + 1)
                ts(gm[:, h, :], bank(2 * h), 7.0, None, ALU.min).then_inc(s_gm[h], 1)
                ts(up1[:, h, :], bank(2 * h + 1), 7.0, -7.0, ALU.min, ALU.max)
                dve.drain()
                stt(up1[:, h, :], up1[:, h, :], 1.0, gm[:, h, :], ALU.add, ALU.mult)
                dve.drain()
                dve.wait_ge(s_sg[h], i + 1)
                tt(actv[:, h, :], up1[:, h, :], sg[:, h, :], ALU.mult).then_inc(s_act[h], 1)

            def dve_block(i):
                dve.wait_ge(s_dn, i + 1)
                ts(bsel[:, :], i_pmod[0:3 * E, :].to_broadcast((3 * E, P)), bexp[0:3 * E, bass.ds(i, 1)], None,
                   ALU.is_equal).then_inc(s_bsel, 1)
                nc.vector.tensor_copy(gate0, gate1)
                nc.vector.tensor_copy(row0[:, :], row1[:, :])
                dve.drain()
                nc.vector.tensor_copy(gate1, slotn[:, 2:3])
                nc.vector.tensor_copy(row1[:, :], rown[:, 1:2])
                dve.drain()
                dve.wait_ge(s_idx, i + 3)
                dve.wait_ge(s_gath, 16 * i + 32)
                slot_rows(bass.ds(i + 2, 1))
                select_slots(bass.ds(i + 3, 1))
                with dve.If(small(i) > 0):
                    swiglu(i, 0)
                    dve.drain().then_inc(s_gm[1], 1)
                    dve.drain().then_inc(s_act[1], 1)
                with dve.Else():
                    for h in range(2):
                        swiglu(i, h)
                dve.wait_ge(s_xt, i + 2)
                with dve.If(small(i + 1) > 0):
                    x_small()
                with dve.Else():
                    x_large()
                dve.wait_ge(s_y, i + 1)
                dve.wait_ge(s_scat, 16 * i + 16)
                nc.vector.tensor_copy(gcur, gate0)
                nc.vector.tensor_copy(rowc[:, :], row0[:, :])
                dve.drain().then_inc(s_cur, 1)

            select_slots(slice(0, 1))
            dve.wait_ge(s_idx, 1)
            slot_rows(slice(0, 1))
            select_slots(slice(1, 2))
            nc.vector.tensor_copy(gate1, slotn[:, 2:3])
            nc.vector.tensor_copy(row1[:, :], rown[:, 1:2])
            nc.vector.memset(gate0, 0.0)
            xj = i_ext.rearrange("p (j o) -> p j o", o=1).to_broadcast((P, EXTRA, E))
            tt(cnt, exst, nbx, ALU.add)
            dve.drain()
            tt(extab[0], xj, exst.rearrange("p (o e) -> p o e", o=1).to_broadcast((P, EXTRA, E)), ALU.is_ge)
            tt(extab[1], xj, cnt.rearrange("p (o e) -> p o e", o=1).to_broadcast((P, EXTRA, E)), ALU.is_lt)
            dve.drain()
            tt(extab[0], extab[0], extab[1], ALU.mult)
            dve.drain()
            tt(extab[0], extab[0], i_exp.rearrange("p (o e) -> p o e", o=1).to_broadcast((P, EXTRA, E)), ALU.mult)
            dve.drain()
            nc.vector.memset(bexp, 0.0)
            dve.drain()
            nc.vector.reduce_sum(bexp[:, E:E + EXTRA], extab[0], AX.X)
            nc.vector.tensor_copy(bexp[:, 0:E], i_exp)
            dve.drain()
            nc.vector.tensor_copy(ints[:, 0:EXTRA], bexp[:, E:E + EXTRA])
            dve.drain().then_inc(extra_known, 1)
            dve.wait_ge(s_idx, 2)
            dve.wait_ge(s_gath, 16)
            slot_rows(slice(1, 2))
            select_slots(slice(2, 3))
            dve.wait_ge(s_xt, 1)
            with dve.If(small(0) > 0):
                x_small()
            with dve.Else():
                x_large()
            n_extra = dve.value_load(ints[0:1, EXTRA:EXTRA + 1], min_val=0, max_val=EXTRA - 1)
            with dve.Fori(0, E) as i:
                dve_block(i)
            with dve.If(n_extra > 0):
                with dve.Fori(0, n_extra) as j:
                    dve_block(j + E)
            def final_norm(a):
                dve.wait_ge(root3_done, a + 1)
                nc.vector.reciprocal(rs[:, a:a + 1], rs[:, a:a + 1])
                dve.drain()
                stt(xr[:, a, :], xr[:, a, :], rs[:, a:a + 1], gfin, ALU.mult, ALU.mult).then_inc(fin_ready, 1)

            dve.wait_ge(ld_gf, 16)
            for a in range(NT):
                xs = xr[:, a, :]
                yr = [ring[:, a * 4096 + n * 1024:a * 4096 + (n + 1) * 1024] for n in range(TOPK)]
                dve.wait_ge(ld_y[a], 16)
                tt(yr[0], yr[0], yr[1], ALU.add)
                tt(yr[2], yr[2], yr[3], ALU.add)
                dve.drain()
                tt(yr[0], yr[0], yr[2], ALU.add)
                dve.drain()
                tt(xs, xs, yr[0], ALU.add).then_inc(sum_ready, 1)
                if a > 0:
                    final_norm(a - 1)
            final_norm(NT - 1)

        @block.tensor
        def _(pe):
            mm = nc.tensor.matmul

            pe.sem_inc(s_dn, 1)
            pe.wait_ge(ld_par, 96)
            for a in range(NT):
                pe.wait_ge(h_ready, a + 1)
                for k in range(KD):
                    last = nc.tensor.transpose(bank(k, a * P, (a + 1) * P), xa[:, a, k * P:(k + 1) * P], ident)
                    if a == NT - 1:
                        last.then_inc(full[fill(("hT", k))], 1)
            for b in range(KD):
                pe.wait_ge(free[b], 1)

            def head_sums(kind, j, src):
                b = fill((kind, j))
                mm(bank(b), head_ones, src, start=True, stop=True).then_inc(full[b], 1)

            def scan_mean(cp):
                b = fill(("mean", cp))
                mm(bank(b), head_ones, oT[:, :, cp * P:(cp + 1) * P], start=True, stop=True).then_inc(full[b], 1)

            def packed_sums(out, src):
                for j in range(NJ):
                    last = mm(out, mats[:, M_PACK + j, :], src(j), start=(j == 0), stop=(j == NJ - 1))
                return last

            def scan_squares_sum(cp):
                pe.wait_ge(gnsq_ready, cp + 1)
                b = fill(("var", cp))
                packed_sums(bank(b, 0, P), lambda j: tmpo[:, j, cp * P:(cp + 1) * P]).then_inc(full[b], 1)

            def scan_spread(cp):
                pe.wait_ge(gninv_ready, cp + 1)
                b = fill(("spread", cp))
                for j in range(NJ):
                    last = mm(bank(b, j * P, (j + 1) * P), mats[:, M_SPREAD + j, :], scan_rms[:, cp * P:(cp + 1) * P],
                              start=True, stop=True)
                last.then_inc(full[b], 1)

            def gate_product(cp):
                b = fill(("g", cp))
                for j in range(NJ):
                    last = mm(bank(b, j * P, (j + 1) * P), wup[:, 1, j * P:(j + 1) * P],
                              pT[:, Q_G, cp * P:(cp + 1) * P], start=True, stop=True)
                last.then_inc(full[b], 1)

            for g in range(NG):
                if g == LORA_AT:
                    pe.wait_ge(lora_in, 1)
                    for kind, rows in (("w", slice(0, 64)), ("a", slice(64, 128))):
                        for j in range(NJ):
                            b = fill((kind, j))
                            mm(bank(b), wup[rows, 0, j * P:(j + 1) * P], pT[rows, Q_WA, :], start=True,
                               stop=True).then_inc(full[b], 1)
                if g == NORM_AT:
                    pe.wait_ge(kksq_ready, 1)
                    for j in range(NJ):
                        head_sums("kk", j, dbuf[:, j, :])
                    pe.wait_ge(rk_ready, 1)
                    for j in range(NJ):
                        head_sums("bonus", j, bonus[:, j, :])
                pe.wait_ge(ld_w[g % 4], 16 * (g // 4 + 1))
                for q in range(g * GQ, (g + 1) * GQ):
                    b = fill(("p", q))
                    m0 = (q - g * GQ) * P
                    for k in range(KD):
                        last = mm(bank(b), wbuf[g % 4][:, k, m0:m0 + P], hT[:, k, :], start=(k == 0), stop=(k == KD - 1))
                    if q % GQ == GQ - 1:
                        pe.drain().then_inc(w_used[g % 4], 1)
                    last.then_inc(full[b], 1)

            pe.wait_ge(ld_pack, 16)
            rt_, kt_, v_ = pT[:, Q_R:Q_R + 4, :], pT[:, Q_K:Q_K + 4, :], pT[:, Q_V:Q_V + 4, :]
            pe.wait_ge(cm_ready, 1)
            pe.wait_ge(init_done, 2)
            for cp in range(NCP):
                cols = slice(cp * P, (cp + 1) * P)
                for n, src in enumerate((at, bt, kt_, v_)):
                    b = fill(("tm", cp, n))
                    for j in range(NJ):
                        last = nc.tensor.transpose(bank(b, j * P, (j + 1) * P), src[:, j, cols], ident)
                    last.then_inc(full[b], 1)
                for name, left, right in (("L1", at, bt), ("LT", bt, at), ("MT", kt_, at), ("QB", bt, rt_),
                                          ("QK", kt_, rt_)):
                    for par in range(2):
                        b = fill((name, cp, par))
                        ch = slice(par * 64, par * 64 + 64)
                        for j in range(NJ):
                            last = mm(bank(b, j * P, (j + 1) * P), left[ch, j, cols], right[ch, j, cols],
                                      start=True, stop=True)
                        last.then_inc(full[b], 1)
                if cp > 0:
                    scan_mean(cp - 1)
                for lev in range(NLEV):
                    pe.wait_ge(lb_ready, cp * NLEV + lev + 1)
                    for par in range(2):
                        pe.wait_ge(u_ready, cp * 2 * (NLEV + 1) + 2 * lev + (2 if lev == 0 else par + 1))
                        b = fill(("X", cp, lev, par))
                        for j in range(NJ):
                            s = par * 4 + j
                            last = mm(bank(b, j * P, (j + 1) * P), LB[:, s, :], UI[:, s, :], start=True, stop=True)
                        last.then_inc(full[b], 1)
                    for par in range(2):
                        pe.wait_ge(t_ready, cp * 2 * NLEV + 2 * lev + (2 if lev == 0 else par + 1))
                        pe.wait_ge(x_ready, 2 * (cp * NLEV + lev) + par + 1)
                        b = fill(("U", cp, lev, par))
                        for j in range(NJ):
                            s = par * 4 + j
                            last = mm(bank(b, j * P, (j + 1) * P), TI[:, s, :], XI[:, s, :], start=True, stop=True)
                        last.then_inc(full[b], 1)
                    if cp > 0 and lev == 0:
                        scan_squares_sum(cp - 1)
                    if cp > 0 and lev == 3:
                        scan_spread(cp - 1)
                    for j in conv_spread(cp, lev):
                        pe.wait_ge(conv_rec, 1)
                        b = fill(("conv_spread", j))
                        mm(bank(b), mats[:, M_SPREAD + j, :], conv_rms, start=True, stop=True).then_inc(full[b], 1)
                pe.wait_ge(m_ready, cp + 1)
                pe.wait_ge(tm_ready, 4 * cp + 4)
                b = fill(("mv", cp))
                for h in range(NH):
                    last = mm(bank(b, h * 64, h * 64 + 64), MT[:, slot(h), :], vtm[:, h * 64:h * 64 + 64],
                              start=True, stop=True)
                last.then_inc(full[b], 1)
                pe.wait_ge(u_ready, (cp + 1) * 2 * (NLEV + 1))
                b = fill(("wt", cp))
                for h in range(NH):
                    last = mm(psum[(h % 2) * 64:(h % 2) * 64 + 64, b * 512 + (h // 2) * P:b * 512 + (h // 2 + 1) * P],
                              atm[:, h * 64:h * 64 + 64], UI[:, slot(h), :], start=True, stop=True)
                last.then_inc(full[b], 1)
                pe.wait_ge(mv_ready, cp + 1)
                b = fill(("u0", cp))
                for h in range(NH):
                    last = mm(bank(b, h * 64, h * 64 + 64), UI[:, slot(h), :], mv[:, h * 64:h * 64 + 64],
                              start=True, stop=True)
                last.then_inc(full[b], 1)
                pe.wait_ge(wt_ready, cp + 1)
                o_bank = fill(("o", cp))

                def out_of_state(c):
                    for j in range(NJ):
                        off = o_bank * 512 + j * P + (c % 2) * C
                        mm(psum[:, off:off + C], state[c % 3][:, j, :], rt_[:, j, c * C:(c + 1) * C],
                           start=False, stop=False, skip_group_check=True)

                def out_of_frames(left, right, start):
                    for h in range(NH):
                        last = mm(psum[(h % 2) * 64:(h % 2) * 64 + 64, o_bank * 512 + h // 2 * P:o_bank * 512 + h // 2 * P + P],
                                  left[:, h * 64:h * 64 + 64], right[:, slot(h), :], start=start and h < 2, stop=not start,
                                  skip_group_check=True)
                    return last

                for c in (2 * cp, 2 * cp + 1):
                    rc = (c % 2) * C
                    rows = slice(rc, rc + C)
                    if c > 0:
                        pe.wait_ge(st_ready, c)
                    b = fill(("sa", c))
                    for j in range(NJ):
                        last = mm(psum[rows, b * 512 + j * P:b * 512 + (j + 1) * P],
                                  wt[:, j * P + rc:j * P + rc + C], state[c % 3][:, j, :], start=True, stop=True)
                    last.then_inc(full[b], 1)
                    if c == 2 * cp:
                        out_of_frames(vtm, QK, True)
                    out_of_state(c)
                    pe.wait_ge(sa_ready, c + 1)
                    if c == NCH - 1:
                        break
                    b = fill(("st", c))
                    for j in range(NJ):
                        js = slice(j * P, (j + 1) * P)
                        mm(bank(b, j * P, (j + 1) * P), ktm[rows, js], vtm[rows, js], start=True, stop=False)
                        last = mm(bank(b, j * P, (j + 1) * P), btm[rows, js], sa[rows, js], start=False, stop=True)
                    last.then_inc(full[b], 1)
                    if c == 2 * cp:
                        if cp == CONV_SUM_AT:
                            pe.wait_ge(conv_y, NJ)
                            b = fill(("conv",))
                            packed_sums(bank(b), lambda j: pT[:, Q_C + j, :]).then_inc(full[b], 1)
                        if cp > 0:
                            gate_product(cp - 1)
                out_of_frames(sa, QB, False).then_inc(full[o_bank], 1)
            def project(a, n):
                b = fill(("x2", a, n))
                for k in range(KD):
                    last = mm(bank(b), y_tiles[k][:, a * P:(a + 1) * P], wout_sb[:, k, n * 512:(n + 1) * 512],
                              start=(k == 0), stop=(k == KD - 1))
                last.then_inc(full[b], 1)

            pe.wait_ge(o_ready, NCP)
            scan_mean(last_cp)
            pe.wait_ge(ld_wout, 16)
            pe.wait_ge(conv_done, NJ)
            pe.wait_ge(y_ready, last_cp)
            project(0, 0)
            scan_squares_sum(last_cp)
            project(0, 1)
            gate_product(last_cp)
            scan_spread(last_cp)

            def transpose_h2(a):
                pe.wait_ge(h2_ready, a + 1)
                for n in range(2):
                    b = fill(("h2T", a, n))
                    for k in range(4):
                        kk = 4 * n + k
                        last = nc.tensor.transpose(bank(b, k * P, (k + 1) * P), h2[:, a, kk * P:(kk + 1) * P], ident)
                    last.then_inc(full[b], 1)

            def logits(a):
                pe.wait_ge(h2T_ready, a + 1)
                b = fill(("lgT", a))
                for k in range(KD):
                    last = mm(psum[0:E, b * 512:b * 512 + P], wr_sb[:, k, :], h2T[:, k, a * P:(a + 1) * P],
                              start=(k == 0), stop=(k == KD - 1))
                last.then_inc(full[b], 1)

            pe.wait_ge(ld_wr, 16)
            for a in range(1, NT):
                if a == last_cp:
                    pe.wait_ge(y_ready, NCP)
                for n in range(2):
                    project(a, n)
                for m in after_x2(a):
                    transpose_h2(m)
                    logits(m)
            pe.wait_ge(lgT_ready, NT)
            b = fill(("lg",))
            for a in range(NT):
                last = nc.tensor.transpose(bank(b, a * E, (a + 1) * E), lgts[:, a * P:(a + 1) * P],
                                           mats[0:E, M_ID, 0:E])
            last.then_inc(full[b], 1)
            pe.wait_ge(sel_ready, 1)
            for name, left, right in (("rank", mats[:, M_TRI, :], sel), ("cnt", ones, psel)):
                b = fill((name,))
                mm(bank(b, 0, NS), left, flat(right), start=True, stop=True).then_inc(full[b], 1)

            def small(i):
                return pe.value_load(ints[0:1, bass.ds(i + 32, 1)], min_val=0, max_val=1)

            def slot_index():
                for a in range(NT):
                    last = mm(bank(6, 0, 4), sel4[:, a, :], slotd[:, a, :], start=(a == 0), stop=(a == NT - 1))
                last.then_inc(s_idx, 1)

            def transpose_x(chunks):
                for k in range(chunks):
                    last = nc.tensor.transpose(bank(7 - k // 4, (k % 4) * P, (k % 4 + 1) * P),
                                               xg[:, k * P:(k + 1) * P], ident)
                last.then_inc(s_xt, 1)

            def gate_up(i, h):
                for k in range(KD):
                    if h == 0:
                        pe.wait_ge(gu_in[k], 16 * i + 16)
                    for n in range(2):
                        last = mm(bank(2 * h + n), xiT[:, k, :], wgu_sb[:, k, n * FF + h * 512:n * FF + h * 512 + 512],
                                  start=(k == 0), stop=False)
                    if h == 1:
                        last.then_inc(gu_used[k], 1)
                if h == 0:
                    pe.wait_ge(s_bsel, i + 1)
                for n in range(2):
                    c0 = n * FF + h * 512
                    last = mm(bank(2 * h + n), bsel[:, :], bparts[:, c0:c0 + 512], start=False, stop=True)
                last.then_inc(s_gu[h], 1)

            def side(f, b):
                return psum[f * HALF:(f + 1) * HALF, b * 512:(b + 1) * 512]

            def gate_up_small(i):
                for k in range(KD):
                    pe.wait_ge(gu_in[k], 16 * i + 16)
                    for n in range(2):
                        for f in range(2):
                            c0 = n * FF + f * 512
                            last = mm(side(f, n), xiT[:, k, 0:HALF], wgu_sb[:, k, c0:c0 + 512], start=(k == 0),
                                      stop=False, skip_group_check=True)
                    last.then_inc(gu_used[k], 1)
                pe.wait_ge(s_bsel, i + 1)
                for n in range(2):
                    for f in range(2):
                        c0 = n * FF + f * 512
                        last = mm(side(f, n), bsel[:, 0:HALF], bparts[:, c0:c0 + 512], start=False, stop=True,
                                  skip_group_check=True)
                    last.then_inc(s_gu[1 - n], 1)

            def transpose_act(h):
                for k in range(4):
                    last = nc.tensor.transpose(bank(2 * h, k * P, (k + 1) * P), actv[:, h, k * P:(k + 1) * P], ident)
                    if k < 3:
                        first = last
                last.then_inc(s_at[h], 1)
                return first

            def down(i, ks):
                for k in ks:
                    pe.wait_ge(dn_in[k], 16 * i + 16)
                    for n in range(2):
                        last = mm(bank(4 + n), actT[:, k, :], wdn_sb[:, k, n * 512:(n + 1) * 512], start=False,
                                  stop=(k == KD - 1))
                    last.then_inc(dn_used[k] if k < KD - 1 else s_dn, 1)

            def down_large(i):
                pe.wait_ge(s_act[0], i + 2)
                transpose_act(0)
                pe.wait_ge(s_y, i + 1)
                for n in range(2):
                    c0 = 2 * FF + n * 512
                    mm(bank(4 + n), bsel[:, :], bparts[:, c0:c0 + 512], start=True, stop=False)
                pe.wait_ge(s_ate[0], i + 1)
                down(i, range(0, 2))
                pe.wait_ge(s_act[1], i + 2)
                transpose_act(1)
                down(i, range(2, 4))
                pe.wait_ge(s_ate[1], i + 1)
                down(i, range(4, KD))

            def down_small(i):
                pe.wait_ge(s_act[0], i + 2)
                transpose_act(0).then_inc(s_at[1], 1)
                pe.wait_ge(s_y, i + 1)
                for f in range(2):
                    c0 = 2 * FF + f * 512
                    mm(side(f, 4), bsel[:, 0:HALF], bparts[:, c0:c0 + 512], start=True, stop=False,
                       skip_group_check=True)
                pe.wait_ge(s_ate[0], i + 1)
                for k in range(KD):
                    pe.wait_ge(dn_in[k], 16 * i + 16)
                    for f in range(2):
                        last = mm(side(f, 4), actT[:, k, 0:HALF], wdn_sb[:, k, f * 512:(f + 1) * 512], start=False,
                                  stop=(k == KD - 1), skip_group_check=True)
                    last.then_inc(dn_used[k] if k < KD - 1 else s_dn, 1)

            def pe_block(i, can_be_small):
                pe.wait_ge(s_xti, i + 1)
                pe.wait_ge(s_sel, i + 3)
                slot_index()
                pe.wait_ge(s_act[0], i + 1)
                pe.wait_ge(s_act[1], i + 1)
                if can_be_small:
                    this_small = small(i)
                    with pe.If(this_small > 0):
                        gate_up_small(i)
                    with pe.Else():
                        for h in range(2):
                            gate_up(i, h)
                else:
                    for h in range(2):
                        gate_up(i, h)
                pe.wait_ge(s_row, i + 3)
                pe.wait_ge(s_gath, 16 * i + 32)
                if can_be_small:
                    with pe.If(small(i + 1) > 0):
                        transpose_x(4)
                    with pe.Else():
                        transpose_x(8)
                    with pe.If(this_small > 0):
                        down_small(i)
                    with pe.Else():
                        down_large(i)
                else:
                    transpose_x(8)
                    down_large(i)

            pe.wait_ge(bias_ready, 1)
            pe.wait_ge(routed, 1)
            n_extra = pe.value_load(ints[0:1, EXTRA:EXTRA + 1], min_val=0, max_val=EXTRA - 1)
            pe.wait_ge(s_sel, 1)
            slot_index()
            pe.wait_ge(s_sel, 2)
            pe.wait_ge(s_row, 1)
            slot_index()
            pe.wait_ge(s_gath, 16)
            pe.wait_ge(s_row, 2)
            with pe.If(small(0) > 0):
                transpose_x(4)
            with pe.Else():
                transpose_x(8)
            with pe.Fori(0, E) as i:
                pe_block(i, True)
            with pe.If(n_extra > 0):
                with pe.Fori(0, n_extra) as j:
                    pe_block(j + E, False)


def tables():
    import numpy as np

    s, t = np.arange(P)[:, None], np.arange(P)[None, :]
    same = s // C == t // C
    m = np.zeros((P, M_N, P), np.float32)
    m[:, M_ID] = s == t
    m[:, M_HEAD] = same
    m[:, M_STRICT] = same & (s < t)
    m[:, M_INCL] = same & (s <= t)
    m[:, M_TRI] = s < t
    m[:, M_ONE] = 1
    m[:, M_L1UP] = (s // 2 == t // 2) & (s < t)
    for n, b in enumerate(LEVELS):
        m[:, M_LEV + n] = (s // (2 * b) == t // (2 * b)) & (s % (2 * b) >= b) & (t % (2 * b) < b)
    for j in range(4):
        m[:, M_PACK + j] = t // 16 == 2 * j + s // 64
        m[:, M_SPREAD + j] = s == 16 * (2 * j + t // 64)
    io = np.zeros((P, 1024), np.float32)
    io[:, 0:64] = np.arange(1, 65)
    io[:, 64:192] = np.arange(1, P + 1)
    io[:, 192:224] = np.arange(E)
    io[:, 224:240] = np.arange(EXTRA)
    io[:, 240:244] = s + P * np.arange(NT)
    io[:, 244:245] = s % E
    io[:, 248:252] = TOPK * (s + P * np.arange(NT))
    io[:, 252:253] = s >= HALF
    io[:, 384:512] = HALF * (np.arange(P) >= HALF)
    io[:, 256:384] = np.arange(P) % E != 0
    io[:, 512:1024] = np.arange(T) % C != 0
    return m, io


def kernel(x, w_in, conv_w, conv_norm_g, rwkv_mu, w0, w_up, a0, a_up, g_up, k_k, k_a, r_k, gn_w, gn_b, w_out,
           norm_mix_g, norm_ffn_g, w_router, b_router, w_gu, b_gu, w_down, b_down, norm_final_g):
    import numpy as np
    import concourse.bacc as bacc
    from concourse.bass_utils import run_bass_kernel_spmd

    def cols(a):
        return np.ascontiguousarray(np.reshape(a, (-1, P)).T)

    mats, iota = tables()
    ordered = np.concatenate([w_in[0][:, 1536:], w_in[0][:, :1536]], axis=1)
    grouped = ordered.reshape(KD, P, NG, GQ * P).transpose(2, 1, 0, 3)
    arrays = {
        "x": np.ascontiguousarray(x[0]),
        "w_in": np.ascontiguousarray(grouped),
        "pcol": np.concatenate([cols(a) for a in (norm_mix_g, norm_ffn_g, conv_w, conv_norm_g, rwkv_mu, w0, a0, k_k,
                                                  k_a, r_k, gn_w, gn_b)], axis=1),
        "consts": mats,
        "iota": iota,
        "wa_up": np.concatenate([w_up[0], a_up[0]], axis=0),
        "g_up": np.ascontiguousarray(g_up[0]),
        "w_out": np.ascontiguousarray(w_out[0]),
        "w_router": np.ascontiguousarray(w_router[0]),
        "b_router": np.reshape(b_router, (E, 1)),
        "w_gu": np.reshape(w_gu, (E * D, 2 * FF)),
        "b_gu": np.ascontiguousarray(b_gu[0]),
        "w_down": np.reshape(w_down, (E * FF, D)),
        "b_down": np.ascontiguousarray(b_down[0]),
        "g_final": np.reshape(norm_final_g, (1, D)),
    }
    nc = bacc.Bacc("TRN2", target_bir_lowering=False, num_devices=1)
    aps = {n: nc.dram_tensor(f"in_{n}", a.shape, mybir.dt.from_np(a.dtype), kind="ExternalInput").ap()
           for n, a in arrays.items()}
    out = nc.dram_tensor("out_y", (T, D), F32, kind="ExternalOutput").ap()
    build(nc, out=out, **aps)
    r = run_bass_kernel_spmd(nc, [{f"in_{n}": a for n, a in arrays.items()}], core_ids=[0])
    return r.results[0]["out_y"].reshape(1, T, D)
```
